# Optimizing a Trainium2 kernel written in Bass

```python
import jax, jax.numpy as jnp
from jax import lax
import numpy as np

D_MODEL = 2048
BATCH = 1
SEQ = 256
DEPTH = 1

CHUNK = 64
Q_BLOCK = 128
MLA_HEADS = 16
QK_NOPE = 128
QK_ROPE = 64
V_HEAD = D_MODEL // MLA_HEADS
Q_LORA = 512
KV_LORA = 256
ROPE_THETA = 10000.0
CONV_CH = 1024
CONV_WIDTH = 31
MEM_LEN = 256
MEM_HEADS = 4
MEM_HEAD_DIM = D_MODEL // MEM_HEADS
D_FF = ((-(-8 * D_MODEL // 3)) + 255) // 256 * 256
N_IN = Q_LORA + KV_LORA + QK_ROPE + 2 * CONV_CH + 2 * D_MODEL
EPS = 1e-6
NEG_INF = -1e30

kernel_name = "hybrid_mla_conformer_gated_block"

def rms_norm(x, g):
    xf = x.astype(jnp.float32)
    y = xf * lax.rsqrt(jnp.mean(xf * xf, axis=-1, keepdims=True) + EPS)
    return (y * g.astype(jnp.float32)).astype(x.dtype)

def layer_norm(x, g, b):
    xf = x.astype(jnp.float32)
    mu = jnp.mean(xf, axis=-1, keepdims=True)
    var = jnp.mean(jnp.square(xf - mu), axis=-1, keepdims=True)
    y = (xf - mu) * lax.rsqrt(var + EPS)
    return (y * g.astype(jnp.float32) + b.astype(jnp.float32)).astype(x.dtype)

def rope_tables(positions, dtype):
    inv_freq = 1.0 / (ROPE_THETA ** (jnp.arange(0, QK_ROPE, 2, dtype=jnp.float32) / QK_ROPE))
    ang = positions.astype(jnp.float32)[..., None] * inv_freq
    return jnp.cos(ang)[:, :, None, :].astype(dtype), jnp.sin(ang)[:, :, None, :].astype(dtype)

def apply_rope(t, cos, sin):
    t1, t2 = jnp.split(t, 2, axis=-1)
    return jnp.concatenate([t1 * cos - t2 * sin, t1 * sin + t2 * cos], axis=-1)

def chunk_causal_attention(q, k, v, scale):
    S = q.shape[1]
    chunk_id = jnp.arange(S) // CHUNK
    outs = []
    for qb in range(S // Q_BLOCK):
        q0 = qb * Q_BLOCK
        kend = q0 + Q_BLOCK
        s = jnp.einsum('bqhd,bkhd->bhqk', q[:, q0:kend], k[:, :kend]).astype(jnp.float32) * scale
        mask = chunk_id[q0:kend, None] >= chunk_id[None, :kend]
        p = jax.nn.softmax(jnp.where(mask, s, NEG_INF), axis=-1).astype(v.dtype)
        outs.append(jnp.einsum('bhqk,bkhd->bqhd', p, v[:, :kend]))
    return jnp.concatenate(outs, axis=1)

def mla_branch(c_q, c_kv, k_rope, cos, sin, norm_cq, w_uq, norm_ckv, w_ukv):
    B, S, _ = c_q.shape
    q = (rms_norm(c_q, norm_cq) @ w_uq).reshape(B, S, MLA_HEADS, QK_NOPE + QK_ROPE)
    q = jnp.concatenate([q[..., :QK_NOPE], apply_rope(q[..., QK_NOPE:], cos, sin)], axis=-1)
    kv = (rms_norm(c_kv, norm_ckv) @ w_ukv).reshape(B, S, MLA_HEADS, QK_NOPE + V_HEAD)
    k_nope, v = kv[..., :QK_NOPE], kv[..., QK_NOPE:]
    k_r = apply_rope(k_rope[:, :, None, :], cos, sin)
    k = jnp.concatenate([k_nope, jnp.broadcast_to(k_r, (B, S, MLA_HEADS, QK_ROPE))], axis=-1)
    o = chunk_causal_attention(q, k, v, (QK_NOPE + QK_ROPE) ** -0.5)
    return o.reshape(B, S, MLA_HEADS * V_HEAD)

def conformer_conv_branch(u_in, b_conv_in, w_dw, b_dw, ln_g, ln_b, w_pw2, b_pw2):
    a, g = jnp.split(u_in + b_conv_in, 2, axis=-1)
    u = a * jax.nn.sigmoid(g)
    u = lax.conv_general_dilated(
        u, w_dw[:, None, :].astype(u.dtype), window_strides=(1,),
        padding=[(CONV_WIDTH - 1, 0)], dimension_numbers=('NWC', 'WIO', 'NWC'),
        feature_group_count=CONV_CH) + b_dw
    u = jax.nn.silu(layer_norm(u, ln_g, ln_b))
    return u @ w_pw2 + b_pw2

def memory_cross_attention(h, mem_n, w_q_mem, w_kv_mem, w_o_mem):
    B, S, _ = h.shape
    q = (h @ w_q_mem).reshape(B, S, MEM_HEADS, MEM_HEAD_DIM)
    kv = (mem_n @ w_kv_mem).reshape(B, mem_n.shape[1], 2, MEM_HEADS, MEM_HEAD_DIM)
    k, v = kv[:, :, 0], kv[:, :, 1]
    s = jnp.einsum('bqhd,bmhd->bhqm', q, k).astype(jnp.float32) * MEM_HEAD_DIM ** -0.5
    p = jax.nn.softmax(s, axis=-1).astype(v.dtype)
    o = jnp.einsum('bhqm,bmhd->bqhd', p, v).reshape(B, S, D_MODEL)
    return o @ w_o_mem

def swiglu(h, w_gate, w_up, w_down):
    return (jax.nn.silu(h @ w_gate) * (h @ w_up)) @ w_down

def setup_inputs(seed: int = 0) -> dict:
    key = jax.random.key(seed)
    ks = jax.random.split(key, 32)
    f32 = jnp.float32
    L = DEPTH

    def w(k, shape, fan_in):
        return jax.random.normal(k, shape, f32) * (fan_in ** -0.5)

    def gain(k, shape):
        return 1.0 + 0.02 * jax.random.normal(k, shape, f32)

    def bias(k, shape):
        return 0.02 * jax.random.normal(k, shape, f32)

    x = jax.random.normal(ks[0], (BATCH, SEQ, D_MODEL), f32)
    mem = jax.random.normal(ks[1], (BATCH, MEM_LEN, D_MODEL), f32)
    offset = jax.random.randint(ks[2], (BATCH, 1), 0, 4096, dtype=jnp.int32)
    positions = (offset + jnp.arange(SEQ, dtype=jnp.int32)[None, :]).astype(jnp.int32)
    return {
        "x": x,
        "mem": mem,
        "positions": positions,
        "norm_mix": gain(ks[3], (L, D_MODEL)),
        "w_in": w(ks[4], (L, D_MODEL, N_IN), D_MODEL),
        "b_conv_in": bias(ks[5], (L, 2 * CONV_CH)),
        "norm_cq": gain(ks[6], (L, Q_LORA)),
        "w_uq": w(ks[7], (L, Q_LORA, MLA_HEADS * (QK_NOPE + QK_ROPE)), Q_LORA),
        "norm_ckv": gain(ks[8], (L, KV_LORA)),
        "w_ukv": w(ks[9], (L, KV_LORA, MLA_HEADS * (QK_NOPE + V_HEAD)), KV_LORA),
        "w_dw": w(ks[10], (L, CONV_WIDTH, CONV_CH), CONV_WIDTH),
        "b_dw": bias(ks[11], (L, CONV_CH)),
        "ln_conv_g": gain(ks[12], (L, CONV_CH)),
        "ln_conv_b": bias(ks[13], (L, CONV_CH)),
        "w_pw2": w(ks[14], (L, CONV_CH, D_MODEL), CONV_CH),
        "b_pw2": bias(ks[15], (L, D_MODEL)),
        "w_o": w(ks[16], (L, D_MODEL, D_MODEL), D_MODEL),
        "norm_cross": gain(ks[17], (L, D_MODEL)),
        "norm_mem": gain(ks[18], (L, D_MODEL)),
        "w_q_mem": w(ks[19], (L, D_MODEL, D_MODEL), D_MODEL),
        "w_kv_mem": w(ks[20], (L, D_MODEL, 2 * D_MODEL), D_MODEL),
        "w_o_mem": w(ks[21], (L, D_MODEL, D_MODEL), D_MODEL),
        "norm_ffn": gain(ks[22], (L, D_MODEL)),
        "w_gate": w(ks[23], (L, D_MODEL, D_FF), D_MODEL),
        "w_up": w(ks[24], (L, D_MODEL, D_FF), D_MODEL),
        "w_down": w(ks[25], (L, D_FF, D_MODEL), D_FF),
        "norm_final": gain(ks[26], (D_MODEL,)),
    }

def reference(x, mem, positions, norm_mix, w_in, b_conv_in, norm_cq, w_uq, norm_ckv, w_ukv,
              w_dw, b_dw, ln_conv_g, ln_conv_b, w_pw2, b_pw2, w_o, norm_cross, norm_mem,
              w_q_mem, w_kv_mem, w_o_mem, norm_ffn, w_gate, w_up, w_down, norm_final):
    cos, sin = rope_tables(positions, x.dtype)
    split_at = [Q_LORA, Q_LORA + KV_LORA, Q_LORA + KV_LORA + QK_ROPE,
                Q_LORA + KV_LORA + QK_ROPE + 2 * CONV_CH,
                Q_LORA + KV_LORA + QK_ROPE + 2 * CONV_CH + D_MODEL]
    for l in range(DEPTH):
        h = rms_norm(x, norm_mix[l])
        c_q, c_kv, k_rope, u_in, gate_a, gate_b = jnp.split(h @ w_in[l], split_at, axis=-1)
        y_a = mla_branch(c_q, c_kv, k_rope, cos, sin, norm_cq[l], w_uq[l], norm_ckv[l], w_ukv[l])
        y_b = conformer_conv_branch(u_in, b_conv_in[l], w_dw[l], b_dw[l], ln_conv_g[l],
                                    ln_conv_b[l], w_pw2[l], b_pw2[l])
        merged = jax.nn.sigmoid(gate_a) * y_a + jax.nn.sigmoid(gate_b) * y_b
        x = x + merged @ w_o[l]
        mem_n = rms_norm(mem, norm_mem[l])
        x = x + memory_cross_attention(rms_norm(x, norm_cross[l]), mem_n,
                                       w_q_mem[l], w_kv_mem[l], w_o_mem[l])
        x = x + swiglu(rms_norm(x, norm_ffn[l]), w_gate[l], w_up[l], w_down[l])
    return rms_norm(x, norm_final)


_drawn_inputs = setup_inputs


def setup_inputs(seed=0):
    import zlib

    import numpy as np

    out = dict(_drawn_inputs(seed))
    spreads = {}
    factors = {'norm_mix': 6.791,
     'b_conv_in': 7.061,
     'norm_cq': 8.0,
     'norm_ckv': 8.0,
     'b_dw': 3.741,
     'ln_conv_g': 6.968,
     'ln_conv_b': 7.746,
     'b_pw2': 4.701,
     'norm_cross': 8.0,
     'norm_mem': 8.0,
     'norm_ffn': 4.021,
     'norm_final': 2.896}
    for name, (base, spread) in spreads.items():
        noise = np.random.default_rng([zlib.crc32(name.encode()), seed]).standard_normal(out[name].shape)
        drawn = base * np.exp(spread * noise) if base else spread * noise
        out[name] = __import__('jax').numpy.asarray(drawn.astype(out[name].dtype))
    for name, factor in factors.items():
        out[name] = (out[name] * factor).astype(out[name].dtype)
    return out
```

```python
import math
from contextlib import ExitStack

import numpy as np
import concourse.bass as bass
from concourse import mybir

F32 = mybir.dt.float32
F32R = mybir.dt.float32r
I32 = mybir.dt.int32
ACT = mybir.ActivationFunctionType
ALU = mybir.AluOpType
AX = mybir.AxisListType
ds = bass.ds

P = 128
TOK = 256
NB = TOK // P
D = 2048
DK = D // P
CH = 512
Q_LORA, KV_LORA, ROPE, NOPE, VH = 512, 256, 64, 128, 128
HEADS, PAIRS = 16, 8
CONV_CH, TAPS = 1024, 31
CT = CONV_CH // P
MEM_HEADS = 4
D_FF = 5632
FK = D_FF // P
EPS = 1e-6
MLA_SCALE = float(NOPE + ROPE) ** -0.5
MEM_SCALE = float(D // MEM_HEADS) ** -0.5
NEG = -1e30
HALF = TOK + P
UQ = 2 * (NOPE + ROPE)
RING = 4
TW = 1024
EARLY_TAPS = 20

COL_KV = Q_LORA
COL_U = Q_LORA + KV_LORA + ROPE
COL_G = COL_U + 2 * CONV_CH

T_A, T_B, T_C = 0, 16, 48
T_E, T_D, T_F = 144, 208, 224
T_G, T_H, T_I, T_J = 256, 288, 320, 496
T_END = 592
C_A, C_B, C_C, C_E, C_D, C_F, C_G, C_H, C_I, C_J = 0, 2, 6, 30, 38, 42, 46, 50, 54, 76
Q_X, Q_CQ, Q_CKV, Q_B, Q_C, Q_M0, Q_LAST, Q_M1 = 0, 4, 5, 6, 10, 17, 19, 20
Q_K, Q_D, Q_F, Q_G, Q_H, Q_I = 22, 26, 30, 34, 42, 46
H_X, H_CQ, H_CKV, H_M0, H_M1, H_D, H_F, H_G, H_H, H_I = 0, 8, 10, 11, 15, 19, 27, 35, 43, 51
S_A, S_B, S_K, S_D, S_F, S_G, S_H, S_I = 0, 2, 6, 10, 14, 18, 22, 26
Z_X, Z_CQ, Z_CKV, Z_MEM, Z_F, Z_H, Z_J = 0, 8, 10, 12, 20, 28, 36
R_X, R_CQ, R_CKV, R_MEM, R_LN, R_CROSS, R_FFN, R_FIN = range(8)

VECS = [("norm_mix", 16), ("norm_cross", 16), ("norm_mem", 16), ("norm_ffn", 16),
        ("b_conv_in", 16), ("norm_cq", 4), ("norm_ckv", 2), ("b_dw", 8), ("ln_conv_g", 8), ("ln_conv_b", 8)]
ROW, _n = {}, 0
for _name, _rows in VECS:
    ROW[_name] = _n
    _n += _rows
NVEC = _n


def program(nc, x, mem, positions, norm_mix, w_in, b_conv_in, norm_cq, w_uq, norm_ckv, w_ukv, w_dw,
            b_dw, ln_conv_g, ln_conv_b, w_pw2, b_pw2, w_o, norm_cross, norm_mem, w_q_mem, w_kv_mem,
            w_o_mem, norm_ffn, w_gate, w_up, w_down, norm_final, out):
    def kview(w):
        return w.rearrange("o (k p) n -> (o p) k n", p=P)

    win_v, wuq_v, wukv_v, wpw_v, wo_v = map(kview, (w_in, w_uq, w_ukv, w_pw2, w_o))
    wq_v, wkv_v, wom_v, wg_v, wu_v, wd_v = map(kview, (w_q_mem, w_kv_mem, w_o_mem, w_gate, w_up, w_down))
    x_v = x.rearrange("o (b p) d -> (o p) b d", p=P)
    mem_v = mem.rearrange("o (b p) d -> (o p) b d", p=P)
    out_v = out.rearrange("o (b p) d -> (o p) b d", p=P)
    vec_dram = dict(norm_mix=norm_mix, norm_cross=norm_cross, norm_mem=norm_mem, norm_ffn=norm_ffn,
                    b_conv_in=b_conv_in, norm_cq=norm_cq, norm_ckv=norm_ckv, b_dw=b_dw,
                    ln_conv_g=ln_conv_g, ln_conv_b=ln_conv_b)

    ctx = ExitStack()
    with ctx:
        def sb(stack, name, shape, dt=F32):
            return stack.enter_context(nc.sbuf_tensor(name, shape, dt))

        def sem(name):
            return ctx.enter_context(nc.semaphore(name))

        ident = sb(ctx, "ident", [P, P])
        vec_rows = sb(ctx, "vec_rows", [P, P])
        vecT = sb(ctx, "vecT", [P, NVEC])
        half_bg = sb(ctx, "half_bg", [P, CT])
        wdwT = sb(ctx, "wdwT", [P, CT, 32])
        mask = sb(ctx, "mask", [P, HALF])
        row_bc = sb(ctx, "row_bc", [P, D])
        stage = sb(ctx, "stage", [P, NB, CH])
        junk = sb(ctx, "junk", [P, CH])
        inv_freq = sb(ctx, "inv_freq", [P, ROPE // 2])
        pos_i = sb(ctx, "pos_i", [P, NB], I32)
        pos_f = sb(ctx, "pos_f", [P, NB])
        ang = sb(ctx, "ang", [P, NB, 32])
        turns = sb(ctx, "turns", [P, 2, NB, 32])
        resid = sb(ctx, "resid", [P, 2, NB, 32])
        trig = sb(ctx, "trig", [P, 2, NB, 32])
        sq = sb(ctx, "sq", [P, 8, NB, 4])
        ssum = sb(ctx, "ssum", [P, 8, NB])
        mean_sq = sb(ctx, "mean_sq", [P, 8, NB])
        rfac = sb(ctx, "rfac", [P, 8, NB])
        half_rx = sb(ctx, "half_rx", [P, NB])
        minus_half = sb(ctx, "minus_half", [P, NB])
        table_out = sb(ctx, "table_out", [P, 1])
        negmax = sb(ctx, "negmax", [P, NB, 2])
        rowsum = sb(ctx, "rowsum", [P, NB, 2])
        rowinv = sb(ctx, "rowinv", [P, NB, 2])
        bn6 = sb(ctx, "bn6", [P, NB, 2, 6])
        bn2 = sb(ctx, "bn2", [P, NB, 2])
        xs = sb(ctx, "xs", [P, NB, D])
        raw = sb(ctx, "raw", [P, RING, TW])
        w_hi = sb(ctx, "w_hi", [P, RING, TW], F32R)
        w_lo = sb(ctx, "w_lo", [P, RING, TW], F32R)

        early = ExitStack()
        gates = sb(early, "gates", [P, NB, 2 * D])
        mixT = [sb(early, f"mixT{j}", [P, DK, TOK], F32R) for j in range(2)]
        cqT = [sb(early, f"cqT{j}", [P, 4, TOK], F32R) for j in range(2)]
        ckvT = [sb(early, f"ckvT{j}", [P, 2, TOK], F32R) for j in range(2)]
        q_tok = sb(early, "q_tok", [P, NB, 2, NOPE + ROPE])
        kv_tok = sb(early, "kv_tok", [P, NB, 2, NOPE + VH])
        qr_tok = sb(early, "qr_tok", [P, NB, 2, ROPE])
        rope_a = sb(early, "rope_a", [P, NB, 2, ROPE])
        rope_b = sb(early, "rope_b", [P, NB, 2, ROPE])
        qnT = sb(early, "qnT", [P, 2, TOK])
        qrT = sb(early, "qrT", [P, TOK])
        knT = sb(early, "knT", [P, 2, TOK])
        krT = sb(early, "krT", [P, TOK])
        probs = sb(early, "probs", [P, 2, HALF])
        probsT = sb(early, "probsT", [P, 2, HALF])
        uT = sb(early, "uT", [P, CT, TAPS - 1 + TOK])
        ln_tok = sb(early, "ln_tok", [P, NB, CONV_CH])
        conv = sb(early, "conv", [P, CT, TOK])
        early.close()
        later = ExitStack()
        crossT = [sb(later, f"crossT{j}", [P, DK, TOK], F32R) for j in range(2)]
        middle = ExitStack()
        oT = [sb(middle, f"oT{j}", [P, DK, TOK], F32R) for j in range(2)]
        memKT = sb(middle, "memKT", [P, DK, TOK])
        memV = sb(middle, "memV", [P, NB, D])
        probs_m = sb(middle, "probs_m", [P, NB, TOK])
        conv_age = ExitStack()
        convT = [sb(conv_age, f"convT{j}", [P, CT, TOK], F32R) for j in range(2)]
        conv_age.close()
        memqT = sb(middle, "memqT", [P, 4, TOK])
        probs_mT = sb(middle, "probs_mT", [P, NB, TOK])
        o_m = sb(middle, "o_m", [P, NB, CH])
        middle.close()
        late = ExitStack()
        actT = [sb(late, f"actT{j}", [P, FK, TOK], F32R) for j in range(2)]
        silu_g = row_bc[:, 0:NB * CH].rearrange("p (b n) -> p b n", b=NB)
        late.close()
        later.close()

        acc = ctx.enter_context(nc.psum_tensor("acc", [P, NB, CH], F32))
        tp = ctx.enter_context(nc.psum_tensor("tp", [P, 2, CH], F32))
        sc = ctx.enter_context(nc.psum_tensor("sc", [P, 2, CH], F32))
        ov = ctx.enter_context(nc.psum_tensor("ov", [P, CH], F32))
        xt = ctx.enter_context(nc.psum_tensor("xt", [P, CH], F32))

        raw_full = [sem(f"raw_full{s}") for s in range(RING)]
        hi_done = sem("hi_done")
        lo_done = sem("lo_done")
        tile_done = sem("tile_done")
        acc0_full = sem("acc0_full")
        acc_free = [sem(f"acc_free{b}") for b in range(NB)]
        stage_full = sem("stage_full")
        turned = sem("turned")
        turned_hi = sem("turned_hi")
        turned_out = [sem(f"turned_out{s}") for s in range(2)]
        square_sum = sem("square_sum")
        ms_ready = sem("ms_ready")
        r_ready = sem("r_ready")
        x_in = [sem(f"x_in{c}") for c in range(4)]
        mem_in, x_back, mix_in, vec_in, wdw_in, pos_in, row_in, gain_in = (sem(n) for n in
            ("mem_in", "x_back", "mix_in", "vec_in", "wdw_in", "pos_in", "row_in", "gain_in"))
        ident_made, consts_made, freq_made, zeros_made = (sem(n) for n in
            ("ident_made", "consts_made", "freq_made", "zeros_made"))
        vec_turned, vec_ready, wdw_turned, wdw_ready = (sem(n) for n in
            ("vec_turned", "vec_ready", "wdw_turned", "wdw_ready"))
        trig_step, angles_ready, trig_ready = sem("trig_step"), sem("angles_ready"), sem("trig_ready")
        sums_step = sem("sums_step")
        half_r_ready = sem("half_r_ready")
        kr_ready = sem("kr_ready")
        kr_step = sem("kr_step")
        g_ready = sem("g_ready")
        q_ready, kv_ready = sem("q_ready"), sem("kv_ready")
        rope_step, rope_ready = sem("rope_step"), sem("rope_ready")
        qr_turned, qr_out = sem("qr_turned"), sem("qr_out")
        scores_ready, scores_read = sem("scores_ready"), sem("scores_read")
        max_ready, exp_done = sem("max_ready"), sem("exp_done")
        inv_ready = sem("inv_ready")
        probs_turned, probs_out = sem("probs_turned"), sem("probs_out")
        pv_done, gated_step, branch_a = sem("pv_done"), sem("gated_step"), sem("branch_a")
        conv_step = sem("conv_step")
        ln_turned, bn_step, ln_ready, ln_back, silu_ready, convT_hi, convT_lo = (sem(n) for n in
            ("ln_turned", "bn_step", "ln_ready", "ln_back", "silu_ready", "convT_hi", "convT_lo"))
        pw_step = sem("pw_step")
        memv_ready = sem("memv_ready")
        m_scores, m_max0, m_max, m_exp, m_inv = (sem(n) for n in
            ("m_scores", "m_max0", "m_max", "m_exp", "m_inv"))
        m_turned, m_out, m_pv, o_ready, o_free = (sem(n) for n in
            ("m_turned", "m_out", "m_pv", "o_ready", "o_free"))
        x_new = sem("x_new")
        silu_done = sem("silu_done")
        x_done = sem("x_done")
        table_loaded = sem("table_loaded")
        gained = sem("gained")
        y_left, y_right, y_out = sem("y_left"), sem("y_right"), sem("y_out")

        def vcol(name, k):
            return vecT[:, ds(k + ROW[name], 1)] if not isinstance(k, int) else \
                vecT[:, ROW[name] + k:ROW[name] + k + 1]

        def cols(start, n):
            return slice(start, start + n) if isinstance(start, int) else ds(start, n)

        flat = "p f b j -> p (f b j)"

        def down_tile(t):
            return (2 * t, 2) if t < 16 else (16 + t, 1) if t < 20 else (2 * t - 4, 2)

        block = ctx.enter_context(nc.Block())

        @block.sync
        def _(sp):
            def tile(base, t, src, kt, n, ahead=0):
                s = t % RING
                if ahead >= 0 and not (isinstance(base, int) and base + t < RING):
                    sp.wait_ge(lo_done, base + (t + ahead - RING + 1))
                dst = raw[:, s, 0:kt * n].rearrange("p (k n) -> p k n", k=kt)
                sp.dma_start(dst, src).then_inc(raw_full[s], 16)

            for t in range(16):
                if t < 8:
                    src, n = win_v[:, 2 * t:2 * t + 2, 0:CH], CH
                else:
                    src, n = win_v[:, 2 * t - 16:2 * t - 14, COL_KV:COL_U], COL_U - COL_KV
                if t % 2 == 0 and t < 8:
                    c = t // 2
                    sp.dma_start(xs[:, :, c * CH:(c + 1) * CH], x_v[:, :, c * CH:(c + 1) * CH])\
                        .then_inc(x_in[c], 16)
                tile(T_A, t, src, 2, n)
            with sp.Fori(0, 2) as i:
                col_a = sp.snap(i * CH + COL_U)
                col_g = sp.snap(i * CH + (COL_U + CONV_CH))
                for t in range(16):
                    k = t % 8
                    tile(i * 16 + T_B, t, win_v[:, 2 * k:2 * k + 2, ds(col_a if t < 8 else col_g, CH)], 2, CH)
            with sp.Fori(0, PAIRS) as i:
                col_gate = sp.snap(i * CH + COL_G)
                col_uq = sp.snap(i * UQ)
                col_ukv = sp.snap(i * CH)
                for t in range(8):
                    tile(i * 12 + T_C, t, win_v[:, 2 * t:2 * t + 2, ds(col_gate, CH)], 2, CH)
                for t in range(2):
                    tile(i * 12 + T_C, 8 + t, wuq_v[:, 2 * t:2 * t + 2, ds(col_uq, UQ)], 2, UQ, ahead=t)
                for t in range(2):
                    tile(i * 12 + T_C, 10 + t, wukv_v[:, t:t + 1, ds(col_ukv, CH)], 1, CH, ahead=-1 if t == 0 else 0)
            for w_v, n_chunks, n_tiles, first in ((wkv_v, 8, 8, T_E), (wpw_v, 4, 4, T_D), (wo_v, 4, 8, T_F),
                                                  (wq_v, 4, 8, T_G), (wom_v, 4, 8, T_H)):
                with sp.Fori(0, n_chunks) as i:
                    col = sp.snap(i * CH)
                    for t in range(n_tiles):
                        tile(i * n_tiles + first, t, w_v[:, 2 * t:2 * t + 2, ds(col, CH)], 2, CH)
            with sp.Fori(0, D_FF // CH) as i:
                col = sp.snap(i * CH)
                for t in range(16):
                    w_v, k = (wg_v, t) if t < 8 else (wu_v, t - 8)
                    tile(i * 16 + T_I, t, w_v[:, 2 * k:2 * k + 2, ds(col, CH)], 2, CH)
            with sp.Fori(0, 4) as i:
                col = sp.snap(i * CH)
                for t in range(24):
                    k, kt = down_tile(t)
                    tile(i * 24 + T_J, t, wd_v[:, k:k + kt, ds(col, CH)], kt, CH)
            for b in range(NB):
                for c, ready, count in ((2, y_right, 2 * b + 1), (0, y_left, 2 * b + 1),
                                        (3, y_right, 2 * b + 2), (1, y_left, 2 * b + 2)):
                    at = slice(c * CH, (c + 1) * CH)
                    sp.wait_ge(ready, count)
                    sp.dma_start(out_v[:, b, at], xs[:, b, at]).then_inc(y_out, 16)
            sp.wait_ge(y_out, 128)

        @block.tensor
        def _(pe):
            mm = nc.tensor.matmul
            turn = nc.tensor.transpose

            def products(base, t, n_tiles, lhs, k0, kt, n, chunk):
                s = t % RING
                first, last = t == 0, t == n_tiles - 1
                pe.wait_ge(lo_done, base + (t + 1))
                for b in range(NB):
                    if first and not (isinstance(chunk, int) and chunk == 0):
                        pe.wait_ge(acc_free[b], chunk)
                    for k in range(kt):
                        hi = lhs[0][:, k0 + k, b * P:(b + 1) * P]
                        lo = lhs[1][:, k0 + k, b * P:(b + 1) * P]
                        whi = w_hi[:, s, k * n:(k + 1) * n]
                        wlo = w_lo[:, s, k * n:(k + 1) * n]
                        o = acc[:, b, 0:n]
                        end = last and k == kt - 1
                        mm(o, lo, whi, start=first and k == 0, stop=False)
                        mm(o, hi, wlo, start=False, stop=False)
                        ins = mm(o, hi, whi, start=False, stop=end)
                    if last and b == 0:
                        ins.then_inc(acc0_full, 1)
                ins.then_inc(tile_done, 1)

            def turn_group(q, bank, blocks):
                if not (isinstance(q, int) and q == 0):
                    pe.wait_ge(turned_out[bank], q)
                for j, src in enumerate(blocks):
                    ins = turn(tp[:, bank, j * P:(j + 1) * P], src, ident[:, :])
                ins.then_inc(turned, 1)

            def turn_stage(q, fills):
                pe.wait_ge(stage_full, fills)
                for g in range(2):
                    turn_group(q, g, [stage[:, b, (2 * g + k) * P:(2 * g + k + 1) * P]
                                      for k in range(2) for b in range(NB)])

            def operand_ready(q):
                pe.wait_ge(turned_out[0], q + 1)
                pe.wait_ge(turned_out[1], q + 1)

            pe.wait_ge(ident_made, 2)
            pe.wait_ge(mix_in, 16)
            turn(xt[:, 0:DK], vec_rows[0:DK, :], ident[0:DK, 0:DK]).then_inc(vec_turned, 1)

            def turn_x(g, q):
                turn_group(q, g % 2, [xs[:, b, (2 * g + k) * P:(2 * g + k + 1) * P]
                                      for k in range(2) for b in range(NB)])

            pe.wait_ge(x_in[0], 16)
            turn_x(0, 0)
            turn_x(1, 0)
            for t in range(8):
                pe.wait_ge(turned_out[t % 2], t // 2 + 1)
                products(T_A, t, 8, mixT, 2 * t, 2, CH, C_A)
                if t + 2 < 8:
                    if t % 2 == 0:
                        pe.wait_ge(x_in[t // 2 + 1], 16)
                    turn_x(t + 2, t // 2 + 1)
            pe.wait_ge(vec_in, 16 * (len(VECS) - 1))
            turn(xt[:, P:P + NVEC], vec_rows[0:NVEC, :], ident[0:NVEC, 0:NVEC]).then_inc(vec_turned, 1)
            pe.wait_ge(wdw_in, 16)
            for j in range(CT):
                ins = turn(sc[:, 0, 32 * j:32 * j + TAPS], ln_tok[0:TAPS, 0, j * P:(j + 1) * P], ident[0:TAPS, 0:TAPS])
            ins.then_inc(wdw_turned, 1)
            for t in range(8, 16):
                pos = t - 8
                pe.wait_ge(lo_done, t + 1)
                for b in range(NB):
                    if pos == 0:
                        pe.wait_ge(acc_free[b], 1)
                    for k in range(2):
                        n = COL_U - COL_KV
                        hi = mixT[0][:, 2 * pos + k, b * P:(b + 1) * P]
                        lo = mixT[1][:, 2 * pos + k, b * P:(b + 1) * P]
                        o = acc[:, b, 0:n]
                        whi = w_hi[:, t % RING, k * n:(k + 1) * n]
                        wlo = w_lo[:, t % RING, k * n:(k + 1) * n]
                        mm(o, lo, whi, start=pos == 0 and k == 0, stop=False)
                        mm(o, hi, wlo, start=False, stop=False)
                        ins = mm(o, hi, whi, start=False, stop=pos == 7 and k == 1)
                    if pos == 7 and b == 0:
                        ins.then_inc(acc0_full, 1)
                ins.then_inc(tile_done, 1)
                if pos == 1:
                    turn_stage(Q_CQ, 2 * (S_A + 1))

            for c in range(4):
                for t in range(8):
                    products(T_B + 8 * c, t, 8, mixT, 2 * t, 2, CH, C_B + c)
                    if t == 1 and c == 0:
                        pe.wait_ge(stage_full, 2 * (S_A + 2))
                        turn_group(Q_CKV, 0, [stage[:, b, k * P:(k + 1) * P] for k in range(2) for b in range(NB)])
                    if t == 3 and c == 0:
                        pe.wait_ge(kr_ready, 1)
                        turn_group(Q_CKV, 1, [qr_tok[:, b, :, :].rearrange("p h d -> p (h d)") for b in range(NB)])
                    if t == 1 and c > 0:
                        turn_stage(Q_B + c - 1, 2 * (S_B + c))

            def attention(t, p, q):
                if t == 0:
                    pe.wait_ge(q_ready, 2 * p + 2)
                    turn_group(q, 0, [q_tok[:, b, h, 0:NOPE] for h in range(2) for b in range(NB)])
                    pe.wait_ge(kv_ready, 2 * p + 2)
                    turn_group(q, 1, [kv_tok[:, b, h, 0:NOPE] for h in range(2) for b in range(NB)])
                if t == 1:
                    pe.wait_ge(rope_ready, p + 1)
                    if not (isinstance(p, int) and p == 0):
                        pe.wait_ge(qr_out, p)
                    for b in range(NB):
                        ins = turn(xt[:, b * P:(b + 1) * P], qr_tok[:, b, :, :].rearrange("p h d -> p (h d)"),
                                   ident[:, :])
                    ins.then_inc(qr_turned, 1)
                if t == 2:
                    operand_ready(q)
                    pe.wait_ge(qr_out, p + 1)
                    if not (isinstance(p, int) and p == 0):
                        pe.wait_ge(probs_out, p)
                    for h in range(2):
                        r0 = h * ROPE
                        for qs, keys, at in ((0, P, 0), (P, TOK, P)):
                            o = sc[:, h, at:at + keys]
                            mm(o, qnT[:, h, qs:qs + P], knT[:, h, 0:keys], start=True, stop=False)
                            ins = mm(o, qrT[r0:r0 + ROPE, qs:qs + P], krT[r0:r0 + ROPE, 0:keys],
                                     start=False, stop=True)
                    ins.then_inc(scores_ready, 1)
                if t == 5:
                    pe.wait_ge(exp_done, 4 * p + 4)
                    pe.wait_ge(scores_read, p + 1)
                    for h in range(2):
                        for j in range(3):
                            ins = turn(sc[:, h, j * P:(j + 1) * P], probs[:, h, j * P:(j + 1) * P], ident[:, :])
                    ins.then_inc(probs_turned, 1)
                if t == 7:
                    pe.wait_ge(probs_out, p + 1)
                    if not (isinstance(p, int) and p == 0):
                        pe.wait_ge(gated_step, p)
                    for h in range(2):
                        mm(ov[:, h * VH:(h + 1) * VH], probsT[:, h, 0:P], kv_tok[:, 0, h, NOPE:],
                           start=True, stop=True)
                        for kb in range(2):
                            ins = mm(ov[:, (2 + h) * VH:(3 + h) * VH], probsT[:, h, (1 + kb) * P:(2 + kb) * P],
                                     kv_tok[:, kb, h, NOPE:], start=kb == 0, stop=kb == 1)
                    ins.then_inc(pv_done, 1)

            def gate_and_pair(i, first, last=False):
                for t in range(8):
                    products(i * 12 + T_C, t, 8, mixT, 2 * t, 2, CH, i * 3 + C_C)
                    if first and t == 1:
                        turn_stage(Q_B + 3, 2 * (S_B + 4))
                    if not first:
                        attention(t, i - 1, i + (Q_C - 1))
                if first:
                    operand_ready(Q_CQ)
                    pe.wait_ge(turned_out[0], Q_CKV + 1)
                for t in range(2):
                    tile_products(i * 12 + T_C, 8 + t, t, 2, cqT, 2 * t, 2, UQ, i * 3 + (C_C + 1))
                    if last and t == 0:
                        turn_x(0, Q_M0)
                        turn_x(1, Q_M0)
                kv_products(i * 12 + T_C, i * 3 + (C_C + 2))
                if last:
                    turn_x(2, Q_M0 + 1)
                    turn_x(3, Q_M0 + 1)

            def kv_products(base, chunk):
                pe.wait_ge(lo_done, base + 12)
                for b in range(NB):
                    pe.wait_ge(acc_free[b], chunk)
                    for k in range(2):
                        hi, lo = (ckvT[j][:, k, b * P:(b + 1) * P] for j in range(2))
                        whi, wlo = w_hi[:, (10 + k) % RING, 0:CH], w_lo[:, (10 + k) % RING, 0:CH]
                        mm(acc[:, b, :], lo, whi, start=k == 0, stop=False)
                        mm(acc[:, b, :], hi, wlo, start=False, stop=False)
                        ins = mm(acc[:, b, :], hi, whi, start=False, stop=k == 1)
                        if b == 1:
                            ins.then_inc(tile_done, 1)
                    if b == 0:
                        ins.then_inc(acc0_full, 1)

            def tile_products(base, t, pos, n_tiles, lhs, k0, kt, n, chunk):
                s = t % RING
                first, last = pos == 0, pos == n_tiles - 1
                pe.wait_ge(lo_done, base + (t + 1))
                for b in range(NB):
                    if first:
                        pe.wait_ge(acc_free[b], chunk)
                    for k in range(kt):
                        hi = lhs[0][:, k0 + k, b * P:(b + 1) * P]
                        lo = lhs[1][:, k0 + k, b * P:(b + 1) * P]
                        o = acc[:, b, 0:n]
                        mm(o, lo, w_hi[:, s, k * n:(k + 1) * n], start=first and k == 0, stop=False)
                        mm(o, hi, w_lo[:, s, k * n:(k + 1) * n], start=False, stop=False)
                        ins = mm(o, hi, w_hi[:, s, k * n:(k + 1) * n], start=False, stop=last and k == kt - 1)
                    if last and b == 0:
                        ins.then_inc(acc0_full, 1)
                ins.then_inc(tile_done, 1)

            gate_and_pair(0, True)
            with pe.Fori(1, PAIRS - 1) as i:
                gate_and_pair(i, False)
            gate_and_pair(PAIRS - 1, False, last=True)

            for t in range(8):
                pe.wait_ge(turned_out[t % 2], (Q_M0 + t // 2 if t < 4 else Q_M1 + t // 2 - 2) + 1)
                products(T_E, t, 8, mixT, 2 * t, 2, CH, C_E)
                if t == 1:
                    attention(0, PAIRS - 1, Q_LAST)
                    attention(1, PAIRS - 1, Q_LAST)
                if t == 2:
                    turn_x(4, Q_M1)
                    turn_x(5, Q_M1)
                    attention(2, PAIRS - 1, Q_LAST)
                if t == 4:
                    turn_x(6, Q_M1 + 1)
                    turn_x(7, Q_M1 + 1)
                if t == 5 or t == 7:
                    attention(t, PAIRS - 1, Q_LAST)
            with pe.Fori(1, 4) as c:
                for t in range(8):
                    products(c * 8 + T_E, t, 8, mixT, 2 * t, 2, CH, c + C_E)
                    if t == 1:
                        turn_stage(c + (Q_K - 1), 2 * c + 2 * S_K)
            for t in range(8):
                products(T_E + 32, t, 8, mixT, 2 * t, 2, CH, C_E + 4)
                if t == 1:
                    turn_stage(Q_K + 3, 2 * (S_K + 4))
                if t == 1:
                    pe.wait_ge(conv_step, CT * TAPS)
                    pe.wait_ge(probs_out, PAIRS)
                    pe.wait_ge(gated_step, PAIRS)
                    for b, banks in ((0, (sc[:, 0, :], sc[:, 1, :])), (1, (ov[:, :], xt[:, :]))):
                        for j in range(CT):
                            ins = turn(banks[j // 4][:, (j % 4) * P:(j % 4 + 1) * P],
                                       conv[:, j, b * P:(b + 1) * P], ident[:, :])
                        ins.then_inc(ln_turned, 1)
                if t == 5:
                    pe.wait_ge(ln_ready, 4)
                    for n, bank in enumerate((sc[:, 0, :], sc[:, 1, :], ov[:, :], xt[:, :])):
                        for k in range(2):
                            for b in range(NB):
                                j = 2 * n + k
                                ins = turn(bank[:, (2 * k + b) * P:(2 * k + b + 1) * P],
                                           ln_tok[:, b, j * P:(j + 1) * P], ident[:, :])
                        ins.then_inc(ln_back, 1)
            with pe.Fori(5, 8) as c:
                for t in range(8):
                    products(c * 8 + T_E, t, 8, mixT, 2 * t, 2, CH, c + C_E)

            def pointwise(c, first):
                for t in range(4):
                    if first and t == 0:
                        pe.wait_ge(convT_lo, 2)
                    products(c * 4 + T_D, t, 4, convT, 2 * t, 2, CH, c + C_D)
                    if t == 2 and not first:
                        turn_stage(c + (Q_D - 1), 2 * c + 2 * S_D)

            pointwise(0, True)
            with pe.Fori(1, 4) as c:
                pointwise(c, False)

            def x_update(c, first, tile0, chunk0, lhs, q0, s0):
                for t in range(8):
                    products(c * 8 + tile0, t, 8, lhs, 2 * t, 2, CH, c + chunk0)
                    if t == 1 and not first:
                        turn_stage(c + (q0 - 1), 2 * c + 2 * s0)

            for t in range(8):
                if t % 2 == 0:
                    operand_ready(Q_D + t // 2)
                products(T_F, t, 8, mixT, 2 * t, 2, CH, C_F)
                if t == 2:
                    turn_stage(Q_D + 3, 2 * (S_D + 4))
            with pe.Fori(1, 4) as c:
                x_update(c, False, T_F, C_F, mixT, Q_F, S_F)

            def mem_attention(t, h, q):
                if t == 0:
                    turn_stage(q, 2 * h + 2 * (S_G + 1))
                if t == 1:
                    operand_ready(q)
                    if not (isinstance(h, int) and h == 0):
                        pe.wait_ge(m_exp, 2 * h)
                    for b in range(NB):
                        for k in range(4):
                            ins = mm(sc[:, 0, b * TOK:(b + 1) * TOK], memqT[:, k, b * P:(b + 1) * P],
                                     memKT[:, cols(h * 4 + k, 1), :].rearrange("p o t -> p (o t)"),
                                     start=k == 0, stop=k == 3)
                    ins.then_inc(m_scores, 1)
                if t == 2:
                    pe.wait_ge(m_exp, 2 * h + 2)
                    if not (isinstance(h, int) and h == 0):
                        pe.wait_ge(m_out, h)
                    for kb in range(2):
                        for b in range(NB):
                            ins = turn(sc[:, 1, (2 * kb + b) * P:(2 * kb + b + 1) * P],
                                       probs_m[:, b, kb * P:(kb + 1) * P], ident[:, :])
                    ins.then_inc(m_turned, 1)
                if t == 3:
                    pe.wait_ge(m_out, h + 1)
                    if not (isinstance(h, int) and h == 0):
                        pe.wait_ge(o_ready, 2 * h)
                    for b, bank in ((0, ov), (1, xt)):
                        for kb in range(2):
                            ins = mm(bank[:, :], probs_mT[:, kb, b * P:(b + 1) * P],
                                     memV[:, kb, cols(h * CH, CH)], start=kb == 0, stop=kb == 1)
                    ins.then_inc(m_pv, 1)
                if t == 4:
                    pe.wait_ge(o_ready, 2 * h + 2)
                    for g in range(2):
                        turn_group(q + 1, g, [o_m[:, b, (2 * g + k) * P:(2 * g + k + 1) * P]
                                              for k in range(2) for b in range(NB)])

            for t in range(8):
                if t % 2 == 0:
                    operand_ready(Q_F + t // 2)
                products(T_G, t, 8, crossT, 2 * t, 2, CH, C_G)
                if t == 1:
                    turn_stage(Q_F + 3, 2 * (S_F + 4))
            with pe.Fori(1, 4) as c:
                for t in range(8):
                    products(c * 8 + T_G, t, 8, crossT, 2 * t, 2, CH, c + C_G)
                    mem_attention(t, c - 1, 2 * c + (Q_G - 2))

            for t in range(8):
                if t % 2 == 0:
                    operand_ready(Q_G + t + 1)
                products(T_H, t, 8, oT, 2 * t, 2, CH, C_H)
                mem_attention(t, 3, Q_G + 6)
            with pe.Fori(1, 4) as c:
                x_update(c, False, T_H, C_H, oT, Q_H, S_H)

            for t in range(8):
                if t % 2 == 0:
                    operand_ready(Q_H + t // 2)
                products(T_I, t, 8, crossT, 2 * t, 2, CH, C_I)
                if t == 1:
                    turn_stage(Q_H + 3, 2 * (S_H + 4))
            for t in range(8):
                products(T_I + 8, t, 8, crossT, 2 * t, 2, CH, C_I + 1)
            with pe.Fori(1, D_FF // CH) as i:
                for t in range(8):
                    products(i * 16 + T_I, t, 8, crossT, 2 * t, 2, CH, 2 * i + C_I)
                    if t == 1:
                        turn_stage(i + (Q_I - 1), 2 * i + 2 * S_I)
                for t in range(8):
                    products(i * 16 + (T_I + 8), t, 8, crossT, 2 * t, 2, CH, 2 * i + (C_I + 1))

            def down(c, first):
                for t in range(24):
                    k, kt = down_tile(t)
                    if first and t == 22:
                        operand_ready(Q_I + 10)
                    products(c * 24 + T_J, t, 24, actT, k, kt, CH, c + C_J)
                    if first and t == 1:
                        turn_stage(Q_I + 10, 2 * (S_I + 11))

            operand_ready(Q_I + 9)
            down(0, True)
            with pe.Fori(1, 4) as c:
                down(c, False)

        @block.scalar
        def _(act):
            fn = nc.scalar.activation

            def split_hi(base, t, width=TW):
                s = t % RING
                act.wait_ge(raw_full[s], base * 4 + (16 * (t // RING) + 16))
                if not (isinstance(base, int) and base + t < RING):
                    act.wait_ge(tile_done, base + (t - RING + 1))
                fn(w_hi[:, s, 0:width], raw[:, s, 0:width], ACT.Copy).then_inc(hi_done, 1)

            def acc_full(b, chunk, last_tile):
                if b == 0:
                    act.wait_ge(acc0_full, chunk + 1)
                else:
                    act.wait_ge(tile_done, last_tile)

            def turned_hi_part(g, count, dst, gain=None, scale=1.0):
                act.wait_ge(turned, count)
                if gain is None:
                    fn(dst[0].rearrange("p k t -> p (k t)"), tp[:, g, :], ACT.Copy, scale=scale)\
                        .then_inc(turned_hi, 1)
                else:
                    for k in range(2):
                        ins = fn(dst[k], tp[:, g, k * TOK:(k + 1) * TOK], ACT.Copy, scale=gain[k])
                    ins.then_inc(turned_hi, 1)

            def sum_squares(n, norm, b, c, src, scale=None):
                if not (isinstance(n, int) and n == 0):
                    act.wait_ge(square_sum, n)
                kw = {} if scale is None else {"scale": scale}
                fn(junk[:, 0:src.shape[-1]], src, ACT.Square,
                   accum_out=sq[:, norm, b, cols(c, 1)], **kw).then_inc(square_sum, 1)

            tables = [0]

            def load_table(function):
                if tables[0]:
                    act.wait_ge(table_loaded, tables[0])
                tables[0] += 1
                fn(table_out[:, :], minus_half[:, 0:1], function).then_inc(table_loaded, 1)

            act.dma_start(vec_rows[0:DK, :], norm_mix.rearrange("o (r p) -> (o r) p", p=P)).then_inc(mix_in, 16)
            act.dma_start(pos_i[:, :], positions.rearrange("o (b p) -> p (o b)", p=P),
                          allow_slow_non_contiguous=True).then_inc(pos_in, 16)

            act.wait_ge(consts_made, 1)
            load_table(ACT.Square)
            act.wait_ge(vec_ready, 1)

            def x_hi(g, name, count):
                turned_hi_part(g % 2, count, [mixT[0][:, 2 * g + k, :] for k in range(2)],
                               gain=[vcol(name, 2 * g + k) for k in range(2)])

            x_hi(0, "norm_mix", 1)
            split_hi(T_A, 0)
            split_hi(T_A, 1)
            x_hi(1, "norm_mix", 2)
            split_hi(T_A, 2)
            split_hi(T_A, 3)
            for t in range(8):
                if t < 6:
                    x_hi(t + 2, "norm_mix", t + 3)
                if t == 7:
                    act.wait_ge(r_ready, R_X + 1)
                    for b in range(NB):
                        acc_full(b, C_A, 8)
                        fn(stage[:, b, :], acc[:, b, :], ACT.Copy, scale=rfac[:, R_X, b:b + 1]).then_inc(stage_full, 1)
                        sum_squares(Z_CQ + b, R_CQ, b, 0, acc[:, b, :], rfac[:, R_X, b:b + 1])
                        act.wait_ge(square_sum, Z_CQ + b + 1)
                        act.sem_inc(acc_free[b], 1)
                split_hi(T_A, t + 4, TW if t < 4 else 2 * (COL_U - COL_KV))
                if t < 4:
                    act.wait_ge(x_in[t], 16)
                    for b in range(NB):
                        sum_squares(Z_X + 2 * t + b, R_X, b, t, xs[:, b, t * CH:(t + 1) * CH])
            for t in range(8):
                if t == 1:
                    act.wait_ge(angles_ready, 1)
                    fn(trig[:, :, :, :].rearrange(flat), resid[:, :, :, :].rearrange(flat), ACT.Sin)\
                        .then_inc(trig_ready, 1)
                if t == 2:
                    act.wait_ge(vec_ready, 2)
                    for g in range(2):
                        turned_hi_part(g, 2 * Q_CQ + g + 1, [cqT[0][:, 2 * g + k, :] for k in range(2)],
                                       gain=[vcol("norm_cq", 2 * g + k) for k in range(2)])
                if t == 7:
                    act.wait_ge(turned, 2 * Q_CQ + 2)
                    for b in range(NB):
                        acc_full(b, C_A + 1, 16)
                        fn(stage[:, b, 0:COL_U - COL_KV], acc[:, b, 0:COL_U - COL_KV], ACT.Copy,
                           scale=rfac[:, R_X, b:b + 1]).then_inc(stage_full, 1)
                        sum_squares(Z_CKV + b, R_CKV, b, 0, acc[:, b, 0:KV_LORA], rfac[:, R_X, b:b + 1])
                        act.wait_ge(square_sum, Z_CKV + b + 1)
                        act.sem_inc(acc_free[b], 1)
                split_hi(T_A, t + 12, TW if t >= 4 else 2 * (COL_U - COL_KV))

            def sigmoid_turned(c, q):
                for g in range(2):
                    act.wait_ge(turned, 2 * q + g + 1)
                    for k in range(2):
                        j = 4 * c + 2 * g + k
                        ins = fn(conv[:, 2 * g + k, :], tp[:, g, k * TOK:(k + 1) * TOK], ACT.Tanh, scale=0.5,
                                 bias=half_bg[:, j:j + 1])
                    ins.then_inc(turned_out[g], 1)

            for c in range(4):
                for t in range(8):
                    if t == 7:
                        q = Q_CKV if c == 0 else Q_B + c - 1
                        act.wait_ge(turned, 2 * q + 2)
                        if c == 0:
                            act.wait_ge(kr_ready, 1)
                        for b in range(NB):
                            acc_full(b, C_B + c, T_B + 8 * c + 8)
                            fn(stage[:, b, :], acc[:, b, :], ACT.Copy, scale=rfac[:, R_X, b:b + 1])\
                                .then_inc(stage_full, 1)
                            act.wait_ge(stage_full, 2 * (S_B + c) + b + 1)
                            act.sem_inc(acc_free[b], 1)
                    split_hi(T_B + 8 * c, t + 4)
                    if c == 0 and t == 2:
                        turned_hi_part(0, 2 * Q_CKV + 1, [ckvT[0][:, k, :] for k in range(2)],
                                       gain=[vcol("norm_ckv", k) for k in range(2)])
                    if c == 0 and t == 4:
                        act.wait_ge(turned, 2 * Q_CKV + 2)
                        fn(krT[:, :], tp[:, 1, 0:TOK], ACT.Copy).then_inc(turned_out[1], 1)
                    if c == 2 and t == 2:
                        act.wait_ge(half_r_ready, 2)
                        sigmoid_turned(0, Q_B + 1)
                    if c == 3 and t < 4:
                        if t == 0:
                            act.wait_ge(mem_in, 64)
                        for b in range(NB):
                            sum_squares(Z_MEM + 2 * t + b, R_MEM, b, t, xs[:, b, t * CH:(t + 1) * CH])

            def attention(t, p, q):
                if t == 0:
                    act.wait_ge(turned, 2 * q + 1)
                    if not (isinstance(p, int) and p == 0):
                        act.wait_ge(scores_ready, p)
                    fn(qnT[:, :, :].rearrange("p h t -> p (h t)"), tp[:, 0, :], ACT.Copy).then_inc(turned_out[0], 1)
                    act.wait_ge(turned, 2 * q + 2)
                    fn(knT[:, :, :].rearrange("p h t -> p (h t)"), tp[:, 1, :], ACT.Copy).then_inc(turned_out[1], 1)
                if t == 1:
                    act.wait_ge(qr_turned, p + 1)
                    fn(qrT[:, :], xt[:, 0:TOK], ACT.Copy).then_inc(qr_out, 1)
                if t == 3:
                    act.wait_ge(max_ready, 2 * p + 2)
                    for h in range(2):
                        for b, (at, keys) in enumerate(((0, P), (P, TOK))):
                            fn(probs[:, h, at:at + keys], probs[:, h, at:at + keys], ACT.Exp,
                               bias=negmax[:, b, h:h + 1], accum_out=rowsum[:, b, h:h + 1]).then_inc(exp_done, 1)
                if t == 5:
                    act.wait_ge(probs_turned, p + 1)
                    if not (isinstance(p, int) and p == 0):
                        act.wait_ge(pv_done, p)
                    fn(probsT[:, :, :], sc[:, :, 0:HALF], ACT.Copy).then_inc(probs_out, 1)

            def gate_and_pair(i, first, last=False):
                for t in range(12):
                    if t == 7:
                        for b in range(NB):
                            acc_full(b, i * 3 + C_C, i * 12 + (T_C + 8))
                            fn(gates[:, b, cols(i * CH, CH)], acc[:, b, :], ACT.Tanh, scale=half_rx[:, b:b + 1])\
                                .then_inc(acc_free[b], 1)
                    if t == 9:
                        if not first:
                            act.wait_ge(turned, 2 * i + (2 * Q_C - 1))
                            act.wait_ge(rope_ready, i)
                        for b in range(NB):
                            acc_full(b, i * 3 + (C_C + 1), i * 12 + (T_C + 10))
                            fn(q_tok[:, b, :, :].rearrange("p h d -> p (h d)"), acc[:, b, 0:UQ], ACT.Copy,
                               scale=rfac[:, R_CQ, b:b + 1]).then_inc(q_ready, 1)
                            act.wait_ge(q_ready, 2 * i + (b + 1))
                            act.sem_inc(acc_free[b], 1)
                    if t == 10:
                        if not first:
                            act.wait_ge(pv_done, i)
                        for b in range(NB):
                            acc_full(b, i * 3 + (C_C + 2), i * 12 + (T_C + 12))
                            fn(kv_tok[:, b, :, :].rearrange("p h d -> p (h d)"), acc[:, b, :], ACT.Copy,
                               scale=rfac[:, R_CKV, b:b + 1]).then_inc(kv_ready, 1)
                            act.wait_ge(kv_ready, 2 * i + (b + 1))
                            act.sem_inc(acc_free[b], 1)
                    width = {8: 2 * UQ, 9: 2 * UQ, 10: CH, 11: CH}.get(t + 4, TW)
                    split_hi(i * 12 + T_C, t + 4, width)
                    if first and t == 2:
                        act.wait_ge(g_ready, 1)
                        sigmoid_turned(1, Q_B + 3)
                    if not first:
                        attention(t, i - 1, i + (Q_C - 1))
                    if last and t == 8:
                        x_hi(0, "norm_mem", 2 * Q_M0 + 1)
                        x_hi(1, "norm_mem", 2 * Q_M0 + 2)
                    if last and t == 11:
                        x_hi(2, "norm_mem", 2 * Q_M0 + 3)
                        x_hi(3, "norm_mem", 2 * Q_M0 + 4)

            act.wait_ge(r_ready, R_CKV + 1)
            gate_and_pair(0, True)
            with act.Fori(1, PAIRS - 1) as i:
                gate_and_pair(i, False)
            gate_and_pair(PAIRS - 1, False, last=True)

            def to_stage(chunk, last_tile, fills, before, norm):
                act.wait_ge(turned, before)
                for b in range(NB):
                    acc_full(b, chunk, last_tile)
                    fn(stage[:, b, :], acc[:, b, :], ACT.Copy, scale=rfac[:, norm, b:b + 1]).then_inc(stage_full, 1)
                    act.wait_ge(stage_full, fills + (b + 1))
                    act.sem_inc(acc_free[b], 1)

            def keys_out(c, q):
                for g in range(2):
                    act.wait_ge(turned, 2 * q + (g + 1))
                    fn(memKT[:, cols(c * 4 + 2 * g, 2), :].rearrange("p k t -> p (k t)"), tp[:, g, :], ACT.Copy)\
                        .then_inc(turned_out[g], 1)

            def values_out(c, chunk, last_tile):
                for b in range(NB):
                    acc_full(b, chunk, last_tile)
                    fn(memV[:, b, cols(c * CH, CH)], acc[:, b, :], ACT.Copy, scale=rfac[:, R_MEM, b:b + 1])\
                        .then_inc(acc_free[b], 1)

            for t in range(8):
                if t == 7:
                    act.wait_ge(r_ready, R_MEM + 1)
                    to_stage(C_E, T_E + 8, 2 * S_K, 2 * (Q_B + 4), R_MEM)
                split_hi(T_E, t + 4)
                if t == 1:
                    attention(0, PAIRS - 1, Q_LAST)
                    attention(1, PAIRS - 1, Q_LAST)
                if t == 2:
                    x_hi(4, "norm_mem", 2 * Q_M1 + 1)
                    x_hi(5, "norm_mem", 2 * Q_M1 + 2)
                if t == 3:
                    attention(3, PAIRS - 1, Q_LAST)
                if t == 4:
                    x_hi(6, "norm_mem", 2 * Q_M1 + 3)
                    x_hi(7, "norm_mem", 2 * Q_M1 + 4)
                if t == 5:
                    attention(5, PAIRS - 1, Q_LAST)
            with act.Fori(1, 4) as c:
                for t in range(8):
                    if t == 7:
                        to_stage(c + C_E, c * 8 + (T_E + 8), 2 * c + 2 * S_K, 2 * c + 2 * Q_K, R_MEM)
                    split_hi(c * 8 + T_E, t + 4)
                    if t == 1:
                        keys_out(c - 1, c + (Q_K - 1))
            for t in range(8):
                if t == 7:
                    values_out(0, C_E + 4, T_E + 40)
                split_hi(T_E + 32, t + 4)
                if t == 1:
                    keys_out(3, Q_K + 3)
                if t == 3:
                    load_table(ACT.Silu)
                if t == 5:
                    for j in range(CT):
                        if j % 2 == 0:
                            act.wait_ge(ln_back, j // 2 + 1)
                        bank = (sc[:, 0, :], sc[:, 1, :], ov[:, :], xt[:, :])[j // 2]
                        ins = fn(conv[:, j, :], bank[:, (j % 2) * TOK:(j % 2 + 1) * TOK], ACT.Silu,
                                 scale=vcol("ln_conv_g", j), bias=vcol("ln_conv_b", j)).then_inc(silu_ready, 1)
                if t == 7:
                    for g in range(2):
                        act.wait_ge(silu_ready, 4 * g + 4)
                        fn(convT[0][:, 4 * g:4 * g + 4, :], conv[:, 4 * g:4 * g + 4, :], ACT.Copy)\
                            .then_inc(convT_hi, 1)
            with act.Fori(5, 8) as c:
                for t in range(8):
                    if t == 7:
                        values_out(c - 4, c + C_E, c * 8 + (T_E + 8))
                    split_hi(c * 8 + T_E, t + 4)

            def merged_hi(c, q, count):
                for g in range(2):
                    turned_hi_part(g, count + (g + 1), [mixT[0][:, cols(c * 4 + 2 * g, 2), :]], scale=0.5)

            def pointwise(c, first):
                for t in range(4):
                    split_hi(c * 4 + T_D, t + 4)
                    if t == 2 and not first:
                        merged_hi(c - 1, None, 2 * c + (2 * Q_D - 2))

            pointwise(0, True)
            with act.Fori(1, 4) as c:
                pointwise(c, False)

            def new_x_hi(c, dst, gain, count):
                for g in range(2):
                    turned_hi_part(g, count + (g + 1), [dst[0][:, cols(c * 4 + (2 * g + k), 1), :]
                                                       .rearrange("p o t -> p (o t)") for k in range(2)],
                                   gain=[vcol(gain, c * 4 + (2 * g + k)) for k in range(2)])

            def x_squares(c, fills, z, norm):
                for b in range(NB):
                    act.wait_ge(stage_full, fills + (b + 1))
                    sum_squares(z + b, norm, b, c, stage[:, b, :])

            def x_update(c, first, tile0, q0, s0, z0, norm, gain):
                for t in range(8):
                    split_hi(c * 8 + tile0, t + 4)
                    if t == 1 and not first:
                        new_x_hi(c - 1, crossT, gain, 2 * c + (2 * q0 - 2))
                    if t == 7:
                        x_squares(c, 2 * c + 2 * s0, 2 * c + z0, norm)

            for t in range(8):
                split_hi(T_F, t + 4)
                if t == 2:
                    merged_hi(3, None, 2 * (Q_D + 3))
                if t == 7:
                    x_squares(0, 2 * S_F, Z_F, R_CROSS)
            with act.Fori(1, 4) as c:
                x_update(c, False, T_F, Q_F, S_F, Z_F, R_CROSS, "norm_cross")

            def mem_attention(t, h, q):
                if t == 0:
                    for g in range(2):
                        act.wait_ge(turned, 2 * q + (g + 1))
                        if g == 0 and not (isinstance(h, int) and h == 0):
                            act.wait_ge(m_scores, h)
                        fn(memqT[:, 2 * g:2 * g + 2, :].rearrange("p k t -> p (k t)"), tp[:, g, :], ACT.Copy)\
                            .then_inc(turned_out[g], 1)
                if t == 1:
                    act.wait_ge(m_max, h + 1)
                    if not (isinstance(h, int) and h == 0):
                        act.wait_ge(m_turned, h)
                        act.wait_ge(m_inv, h)
                    for b in range(NB):
                        fn(probs_m[:, b, :], sc[:, 0, b * TOK:(b + 1) * TOK], ACT.Exp, scale=MEM_SCALE,
                           bias=negmax[:, b, 0:1], accum_out=rowsum[:, b, 0:1]).then_inc(m_exp, 1)
                if t == 3:
                    act.wait_ge(m_pv, h + 1)
                    act.wait_ge(m_inv, h + 1)
                    if not (isinstance(h, int) and h == 0):
                        act.wait_ge(turned, 2 * q)
                    act.wait_ge(o_ready, 2 * h + 1)
                    fn(o_m[:, 1, :], xt[:, :], ACT.Copy, scale=rowinv[:, 1, 0:1]).then_inc(o_ready, 1)
                if t == 4:
                    for g in range(2):
                        turned_hi_part(g, 2 * q + (3 + g), [oT[0][:, cols(h * 4 + 2 * g, 2), :]])

            for t in range(8):
                if t == 7:
                    act.wait_ge(x_new, 4)
                    act.wait_ge(r_ready, R_CROSS + 1)
                    to_stage(C_G, T_G + 8, 2 * S_G, 2 * (Q_F + 4), R_CROSS)
                split_hi(T_G, t + 4)
                if t == 1:
                    new_x_hi(3, crossT, "norm_cross", 2 * (Q_F + 3))
            with act.Fori(1, 4) as c:
                for t in range(8):
                    if t == 7:
                        to_stage(c + C_G, c * 8 + (T_G + 8), 2 * c + 2 * S_G, 4 * c + (2 * Q_G - 2), R_CROSS)
                    split_hi(c * 8 + T_G, t + 4)
                    mem_attention(t, c - 1, 2 * c + (Q_G - 2))

            for t in range(8):
                split_hi(T_H, t + 4)
                mem_attention(t, 3, Q_G + 6)
                if t == 7:
                    x_squares(0, 2 * S_H, Z_H, R_FFN)
            with act.Fori(1, 4) as c:
                x_update(c, False, T_H, Q_H, S_H, Z_H, R_FFN, "norm_ffn")

            def silu_out(chunk, last_tile, n):
                if not (isinstance(n, int) and n == 0):
                    act.wait_ge(stage_full, 2 * n + 2 * S_I)
                for b in range(NB):
                    acc_full(b, chunk, last_tile)
                    fn(silu_g[:, b, :], acc[:, b, :], ACT.Silu, scale=rfac[:, R_FFN, b:b + 1])\
                        .then_inc(silu_done, 1)
                    act.wait_ge(silu_done, 2 * n + (b + 1))
                    act.sem_inc(acc_free[b], 1)

            def act_hi(n, count):
                for g in range(2):
                    turned_hi_part(g, count + (g + 1), [actT[0][:, cols(n * 4 + 2 * g, 2), :]])

            for t in range(16):
                if t == 7:
                    act.wait_ge(r_ready, R_FFN + 1)
                    silu_out(C_I, T_I + 8, 0)
                split_hi(T_I, t + 4)
                if t == 1:
                    new_x_hi(3, crossT, "norm_ffn", 2 * (Q_H + 3))
                    load_table(ACT.Silu)
            with act.Fori(1, D_FF // CH) as i:
                for t in range(16):
                    if t == 7:
                        silu_out(2 * i + C_I, i * 16 + (T_I + 8), i)
                    split_hi(i * 16 + T_I, t + 4)
                    if t == 1:
                        act_hi(i - 1, 2 * i + (2 * Q_I - 2))

            def down(c, first, end):
                for t in range(24):
                    if t + 4 < 24 or not end:
                        split_hi(c * 24 + T_J, t + 4, down_tile((t + 4) % 24)[1] * CH)
                    if first and t == 1:
                        act_hi(10, 2 * (Q_I + 10))
                for b in range(NB):
                    act.wait_ge(x_done, 2 * c + (b + 1))
                    sum_squares(2 * c + (Z_J + b), R_FIN, b, c, xs[:, b, cols(c * CH, CH)])

            down(0, True, False)
            with act.Fori(1, 3) as c:
                down(c, False, False)
            down(3, False, True)
            act.wait_ge(gained, 3)
            for b in range(NB):
                act.wait_ge(r_ready, R_FIN + 1 + b)
                for c in range(2):
                    at = slice(c * CH, (c + 1) * CH)
                    fn(xs[:, b, at], xs[:, b, at], ACT.Copy, scale=rfac[:, R_FIN, b:b + 1]).then_inc(y_left, 1)

        @block.vector
        def _(dve):
            V = nc.vector

            def split_lo(base, t, width=TW):
                s = t % RING
                dve.wait_ge(hi_done, base + (t + 1))
                V.tensor_tensor(w_lo[:, s, 0:width], raw[:, s, 0:width], w_hi[:, s, 0:width].bitcast(F32),
                                ALU.subtract).then_inc(lo_done, 1)

            def acc_full(b, chunk, last_tile):
                if b == 0:
                    dve.wait_ge(acc0_full, chunk + 1)
                else:
                    dve.wait_ge(tile_done, last_tile)

            def turned_lo_part(g, count, dst, gain=None, scale=1.0):
                dve.wait_ge(turned_hi, count)
                if gain is None:
                    V.scalar_tensor_tensor(out=dst[1][0].rearrange("p k t -> p (k t)"), in0=tp[:, g, :], scalar=scale,
                                           in1=dst[0][0].rearrange("p k t -> p (k t)").bitcast(F32),
                                           op0=ALU.mult, op1=ALU.subtract).then_inc(turned_out[g], 1)
                else:
                    for k in range(2):
                        ins = V.scalar_tensor_tensor(out=dst[1][k], in0=tp[:, g, k * TOK:(k + 1) * TOK],
                                                     scalar=gain[k], in1=dst[0][k].bitcast(F32),
                                                     op0=ALU.mult, op1=ALU.subtract)
                    ins.then_inc(turned_out[g], 1)

            sums = [0]

            def mean_square(norm, n, parts, count):
                dve.wait_ge(square_sum, count)
                if parts > 1:
                    V.tensor_reduce(ssum[:, norm, :], sq[:, norm, :, 0:parts], AX.X, ALU.add).then_inc(sums_step, 1)
                    sums[0] += 1
                    dve.wait_ge(sums_step, sums[0])
                    src = ssum[:, norm, :]
                else:
                    src = sq[:, norm, :, 0:1].rearrange("p b o -> p (b o)")
                V.tensor_scalar(mean_sq[:, norm, :], src, 1.0 / n, EPS, ALU.mult, ALU.add).then_inc(ms_ready, 1)

            dve.wait_ge(vec_turned, 1)
            V.tensor_copy(vecT[:, 0:DK], xt[:, 0:DK]).then_inc(vec_ready, 1)
            dve.wait_ge(vec_ready, 1)

            def x_lo(g, name, count):
                turned_lo_part(g % 2, count, [[mixT[j][:, 2 * g + k, :] for k in range(2)] for j in range(2)],
                               gain=[vcol(name, 2 * g + k) for k in range(2)])

            x_lo(0, "norm_mix", 1)
            split_lo(T_A, 0)
            split_lo(T_A, 1)
            x_lo(1, "norm_mix", 2)
            split_lo(T_A, 2)
            split_lo(T_A, 3)
            for t in range(16):
                if t < 6:
                    x_lo(t + 2, "norm_mix", t + 3)
                split_lo(T_A, t + 4, TW if t < 4 or t >= 12 else 2 * (COL_U - COL_KV))
                if t == 4:
                    mean_square(R_X, D, 4, Z_X + 8)
                    dve.wait_ge(r_ready, R_X + 1)
                    V.tensor_scalar(half_rx[:, :], rfac[:, R_X, :], 0.5, None, ALU.mult).then_inc(half_r_ready, 1)
                if t == 8:
                    mean_square(R_CQ, Q_LORA, 1, Z_CQ + 2)
                    dve.wait_ge(vec_turned, 2)
                    V.tensor_copy(vecT[:, DK:], xt[:, P + DK:P + NVEC]).then_inc(vec_ready, 1)
                    dve.wait_ge(vec_ready, 2)
                    V.tensor_scalar(half_bg[:, :], vecT[:, ROW["b_conv_in"] + CT:ROW["b_conv_in"] + 2 * CT], 0.5,
                                    None, ALU.mult).then_inc(half_r_ready, 1)
                    dve.wait_ge(wdw_turned, 1)
                    V.tensor_scalar(wdwT[:, :, 0:TAPS], sc[:, 0, 0:32 * CT].rearrange("p (j w) -> p j w", w=32)[:, :, 0:TAPS],
                                    0.5, None, ALU.mult).then_inc(wdw_ready, 1)
                if t == 10:
                    for g in range(2):
                        turned_lo_part(g, H_CQ + g + 1, [[cqT[j][:, 2 * g + k, :] for k in range(2)] for j in range(2)],
                                       gain=[vcol("norm_cq", 2 * g + k) for k in range(2)])
            def glu_input(c, q):
                for g in range(2):
                    dve.wait_ge(turned, 2 * q + g + 1)
                    for k in range(2):
                        j = 4 * c + 2 * g + k
                        ins = V.tensor_scalar(uT[:, j, TAPS - 1:], tp[:, g, k * TOK:(k + 1) * TOK],
                                              vcol("b_conv_in", j), None, ALU.add)
                    ins.then_inc(turned_out[g], 1)

            def glu(c, q):
                dve.wait_ge(turned_out[0], q + 1)
                dve.wait_ge(turned_out[1], q + 1)
                for j in range(4 * c, 4 * c + 4):
                    ins = V.scalar_tensor_tensor(out=uT[:, j, TAPS - 1:], in0=conv[:, j - 4 * c, :], scalar=1.0,
                                                 in1=uT[:, j, TAPS - 1:], op0=ALU.add, op1=ALU.mult)
                ins.then_inc(g_ready, 1)

            for c in range(4):
                for t in range(8):
                    split_lo(T_B + 8 * c, t + 4)
                    if c == 0 and t == 0:
                        mean_square(R_CKV, KV_LORA, 1, Z_CKV + 2)
                    if c == 0 and t == 2:
                        turned_lo_part(0, H_CKV + 1, [[ckvT[j][:, k, :] for k in range(2)] for j in range(2)],
                                       gain=[vcol("norm_ckv", k) for k in range(2)])
                    if c == 1 and t == 2:
                        glu_input(0, Q_B)
                    if c == 2 and t == 3:
                        glu(0, Q_B + 1)
                    if c == 3 and t == 2:
                        glu_input(1, Q_B + 2)
                    if c == 3 and t == 5:
                        mean_square(R_MEM, D, 4, Z_MEM + 8)

            def taps(j, w0, w1, before):
                for w in range(w0, w1):
                    u = uT[:, cols(j, 1), w:w + TOK].rearrange("p o t -> p (o t)")
                    a = conv[:, cols(j, 1), :].rearrange("p o t -> p (o t)")
                    wt = wdwT[:, cols(j, 1), w:w + 1].rearrange("p o t -> p (o t)")
                    if w == 0:
                        ins = V.tensor_scalar(a, u, wt, vcol("b_dw", j), ALU.mult, ALU.add)
                    else:
                        dve.wait_ge(conv_step, before + (w - w0))
                        ins = V.scalar_tensor_tensor(out=a, in0=u, scalar=wt, in1=a, op0=ALU.mult, op1=ALU.add)
                    ins.then_inc(conv_step, 1)

            def attention(t, p, q):
                if t == 2:
                    dve.wait_ge(scores_ready, p + 1)
                    if not (isinstance(p, int) and p == 0):
                        dve.wait_ge(probs_turned, p)
                    for h in range(2):
                        ins = V.scalar_tensor_tensor(out=probs[:, h, :], in0=sc[:, h, 0:HALF], scalar=MLA_SCALE,
                                                     in1=mask[:, :], op0=ALU.mult, op1=ALU.add)
                    ins.then_inc(scores_read, 1)
                    dve.wait_ge(scores_read, p + 1)
                    for b, (at, keys) in enumerate(((0, P), (P, TOK))):
                        V.tensor_reduce(negmax[:, b, :], probs[:, :, at:at + keys], AX.X, ALU.max, negate=True)\
                            .then_inc(max_ready, 1)
                if t == 3:
                    dve.wait_ge(exp_done, 4 * p + 4)
                    V.reciprocal(rowinv[:, :, :], rowsum[:, :, :]).then_inc(inv_ready, 1)
                if t == 7:
                    dve.wait_ge(pv_done, p + 1)
                    g = gates[:, :, cols(p * (2 * VH), 2 * VH)]
                    V.scalar_tensor_tensor(out=g, in0=g, scalar=1.0,
                                           in1=ov[:, :].rearrange("p (b n) -> p b n", b=NB),
                                           op0=ALU.add, op1=ALU.mult).then_inc(gated_step, 1)
                    dve.wait_ge(gated_step, p + 1)
                    dve.wait_ge(inv_ready, p + 1)
                    for b in range(NB):
                        gb = gates[:, b, cols(p * (2 * VH), 2 * VH)].rearrange("p (h d) -> p h d", h=2)
                        ins = V.tensor_tensor(gb, gb,
                                              rowinv[:, b, :, None].broadcast_to([P, 2, VH]), ALU.mult)
                    ins.then_inc(branch_a, 1)

            share = [0, 0, 2, 3, 4, 6, 8, 10, 12, 14, 16, 18, EARLY_TAPS]
            share_first = [0, 0, 0, 0, 0, 6, 8, 10, 12, 14, 16, 18, EARLY_TAPS]
            share_last = [0, 3, 6, 7, 9, 12, 15, 18, 18, 18, 19, 19, EARLY_TAPS]

            def gate_and_pair(i, first, last=False):
                for t in range(12):
                    width = {8: 2 * UQ, 9: 2 * UQ, 10: CH, 11: CH}.get(t + 4, TW)
                    split_lo(i * 12 + T_C, t + 4, width)
                    if first and t == 3:
                        glu(1, Q_B + 3)
                        dve.wait_ge(g_ready, 2)
                        dve.wait_ge(wdw_ready, 1)
                        dve.wait_ge(zeros_made, 1)
                    if not first:
                        attention(t, i - 1, i + (Q_C - 1))
                    if last and t == 8:
                        x_lo(0, "norm_mem", H_M0 + 1)
                        x_lo(1, "norm_mem", H_M0 + 2)
                    if last and t == 11:
                        x_lo(2, "norm_mem", H_M0 + 3)
                        x_lo(3, "norm_mem", H_M0 + 4)
                    at = share_first if first else share_last if last else share
                    if at[t + 1] > at[t]:
                        taps(i, at[t], at[t + 1], i * EARLY_TAPS + at[t])

            gate_and_pair(0, True)
            with dve.Fori(1, PAIRS - 1) as i:
                gate_and_pair(i, False)
            gate_and_pair(PAIRS - 1, False, last=True)

            LATE = TAPS - EARLY_TAPS
            after_c = CT * EARLY_TAPS

            def late_taps(c, t):
                order = [(half, EARLY_TAPS + w) for half in range(2) for w in range(LATE)]
                lo, hi = (min(len(order), n * 3) for n in (t, t + 1))
                for n in range(lo, hi):
                    half, w = order[n]
                    taps(c * 2 + half, w, w + 1, c * (2 * LATE) + (after_c + n))

            for t in range(8):
                split_lo(T_E, t + 4)
                if t == 2:
                    x_lo(4, "norm_mem", H_M1 + 1)
                    x_lo(5, "norm_mem", H_M1 + 2)
                    attention(2, PAIRS - 1, Q_LAST)
                if t == 3:
                    attention(3, PAIRS - 1, Q_LAST)
                if t == 4:
                    x_lo(6, "norm_mem", H_M1 + 3)
                    x_lo(7, "norm_mem", H_M1 + 4)
                if t == 7:
                    attention(7, PAIRS - 1, Q_LAST)
                late_taps(0, t)
            with dve.Fori(1, 4) as c:
                for t in range(8):
                    split_lo(c * 8 + T_E, t + 4)
                    late_taps(c, t)
            for t in range(8):
                split_lo(T_E + 32, t + 4)
                if t == 1:
                    banks = ((sc[:, 0, :], sc[:, 1, :]), (ov[:, :], xt[:, :]))
                    for b in range(NB):
                        dve.wait_ge(ln_turned, b + 1)
                        for h in range(2):
                            ins = V.bn_stats(bn6[:, b, h, :], banks[b][h])
                        ins.then_inc(bn_step, 1)
                    for b in range(NB):
                        dve.wait_ge(bn_step, b + 1)
                        ins = V.bn_aggr(bn2[:, b, :], bn6[:, b, :, :])
                    ins.then_inc(bn_step, 1)
                    dve.wait_ge(bn_step, 3)
                    V.tensor_scalar(mean_sq[:, R_LN, :], bn2[:, :, 1], EPS, None, ALU.add).then_inc(ms_ready, 1)
                if t == 2:
                    dve.wait_ge(r_ready, R_LN + 1)
                    for b in range(NB):
                        for h in range(2):
                            V.tensor_scalar(ln_tok[:, b, h * CH:(h + 1) * CH], banks[b][h], bn2[:, b, 0:1],
                                            rfac[:, R_LN, b:b + 1], ALU.subtract, ALU.mult).then_inc(ln_ready, 1)
                if t == 7:
                    for g in range(2):
                        dve.wait_ge(convT_hi, g + 1)
                        V.tensor_tensor(convT[1][:, 4 * g:4 * g + 4, :], conv[:, 4 * g:4 * g + 4, :],
                                        convT[0][:, 4 * g:4 * g + 4, :].bitcast(F32), ALU.subtract)\
                            .then_inc(convT_lo, 1)
            with dve.Fori(5, 8) as c:
                for t in range(8):
                    split_lo(c * 8 + T_E, t + 4)

            def bias_added(b, c, chunk, last_tile, free):
                dve.wait_ge(turned, free)
                acc_full(b, chunk, last_tile)
                V.tensor_tensor(stage[:, b, :], acc[:, b, :], row_bc[:, cols(c * CH, CH)], ALU.add)\
                    .then_inc(acc_free[b], 1)

            def merge(c, chunk, before):
                for b in range(NB):
                    dve.wait_ge(acc_free[b], chunk + 1)
                    V.scalar_tensor_tensor(out=stage[:, b, :], in0=gates[:, b, cols(c * CH + D, CH)], scalar=1.0,
                                           in1=stage[:, b, :], op0=ALU.add, op1=ALU.mult).then_inc(pw_step, 1)
                for b in range(NB):
                    dve.wait_ge(pw_step, before + (b + 1))
                    V.tensor_tensor(stage[:, b, :], stage[:, b, :], gates[:, b, cols(c * CH, CH)], ALU.add)\
                        .then_inc(stage_full, 1)

            def merged_lo(c, count):
                for g in range(2):
                    turned_lo_part(g, count + (g + 1),
                                   [[mixT[j][:, cols(c * 4 + 2 * g, 2), :]] for j in range(2)], scale=0.5)

            dve.wait_ge(row_in, 16)
            dve.wait_ge(branch_a, PAIRS)

            def pointwise(c, first, free):
                for t in range(4):
                    split_lo(c * 4 + T_D, t + 4)
                    if t == 2:
                        for b in range(NB):
                            bias_added(b, c, c + C_D, c * 4 + (T_D + 4), free)
                if not first:
                    merged_lo(c - 1, 2 * c + (H_D - 2))
                merge(c, c + C_D, 2 * c)

            pointwise(0, True, 2 * (Q_K + 4))
            with dve.Fori(1, 4) as c:
                pointwise(c, False, 2 * c + 2 * Q_D)

            def new_x_lo(c, gain, count):
                for g in range(2):
                    turned_lo_part(g, count + (g + 1),
                                   [[crossT[j][:, cols(c * 4 + (2 * g + k), 1), :].rearrange("p o t -> p (o t)")
                                     for k in range(2)] for j in range(2)],
                                   gain=[vcol(gain, c * 4 + (2 * g + k)) for k in range(2)])

            def new_x(b, c, chunk, last_tile, fills, free, copied=None, squared=None):
                dve.wait_ge(turned, free)
                if copied is not None:
                    dve.wait_ge(x_new, copied)
                    dve.wait_ge(square_sum, squared)
                acc_full(b, chunk, last_tile)
                V.tensor_tensor(stage[:, b, :], acc[:, b, :], xs[:, b, cols(c * CH, CH)], ALU.add)\
                    .then_inc(stage_full, 1)
                dve.wait_ge(stage_full, fills + (b + 1))
                dve.sem_inc(acc_free[b], 1)

            dve.wait_ge(x_back, 64)
            for t in range(8):
                for b in range(NB) if t == 6 else ():
                    new_x(b, 0, C_F, T_F + 8, 2 * S_F, 2 * (Q_D + 4))
                split_lo(T_F, t + 4)
                if t == 2:
                    merged_lo(3, H_D + 6)
            with dve.Fori(1, 4) as c:
                for t in range(8):
                    for b in range(NB) if t == 6 else ():
                        new_x(b, c, c + C_F, c * 8 + (T_F + 8), 2 * c + 2 * S_F, 2 * c + 2 * Q_F,
                              copied=c, squared=2 * c + Z_F)
                    split_lo(c * 8 + T_F, t + 4)
                    if t == 1:
                        new_x_lo(c - 1, "norm_cross", 2 * c + (H_F - 2))

            def mem_attention(t, h, q):
                if t == 1:
                    dve.wait_ge(m_scores, h + 1)
                    if not (isinstance(h, int) and h == 0):
                        dve.wait_ge(m_exp, 2 * h)
                    V.tensor_reduce(ssum[:, R_LN, :], sc[:, 0, :].rearrange("p (b k) -> p b k", b=NB), AX.X,
                                    ALU.max, negate=True).then_inc(m_max0, 1)
                    dve.wait_ge(m_max0, h + 1)
                    V.tensor_scalar(negmax[:, :, 0], ssum[:, R_LN, :], MEM_SCALE, None, ALU.mult).then_inc(m_max, 1)
                if t == 2:
                    dve.wait_ge(m_exp, 2 * h + 2)
                    if not (isinstance(h, int) and h == 0):
                        dve.wait_ge(o_ready, 2 * h)
                    V.reciprocal(rowinv[:, :, 0], rowsum[:, :, 0]).then_inc(m_inv, 1)
                if t == 2:
                    dve.wait_ge(m_turned, h + 1)
                    if not (isinstance(h, int) and h == 0):
                        dve.wait_ge(m_pv, h)
                    V.tensor_copy(probs_mT[:, :, :].rearrange("p k t -> p (k t)"), sc[:, 1, :]).then_inc(m_out, 1)
                if t == 3:
                    dve.wait_ge(m_pv, h + 1)
                    dve.wait_ge(m_inv, h + 1)
                    if not (isinstance(h, int) and h == 0):
                        dve.wait_ge(turned, 2 * q)
                    V.tensor_scalar(o_m[:, 0, :], ov[:, :], rowinv[:, 0, 0:1], None, ALU.mult).then_inc(o_ready, 1)
                if t == 4:
                    for g in range(2):
                        turned_lo_part(g, 2 * h + (H_G + g + 1), [[oT[j][:, cols(h * 4 + 2 * g, 2), :]] for j in range(2)])

            for t in range(8):
                if t == 0:
                    mean_square(R_CROSS, D, 4, Z_F + 8)
                split_lo(T_G, t + 4)
                if t == 1:
                    new_x_lo(3, "norm_cross", H_F + 6)
            with dve.Fori(1, 4) as c:
                for t in range(8):
                    split_lo(c * 8 + T_G, t + 4)
                    mem_attention(t, c - 1, 2 * c + (Q_G - 2))

            dve.wait_ge(x_new, 4)
            for t in range(8):
                for b in range(NB) if t == 6 else ():
                    new_x(b, 0, C_H, T_H + 8, 2 * S_H, 2 * (Q_G + 8))
                split_lo(T_H, t + 4)
                mem_attention(t, 3, Q_G + 6)
            with dve.Fori(1, 4) as c:
                for t in range(8):
                    for b in range(NB) if t == 6 else ():
                        new_x(b, c, c + C_H, c * 8 + (T_H + 8), 2 * c + 2 * S_H, 2 * c + 2 * Q_H,
                              copied=c + 4, squared=2 * c + Z_H)
                    split_lo(c * 8 + T_H, t + 4)
                    if t == 1:
                        new_x_lo(c - 1, "norm_ffn", 2 * c + (H_H - 2))

            def gated_up(b, n, chunk, last_tile, free):
                dve.wait_ge(turned, free)
                dve.wait_ge(silu_done, 2 * n + (b + 1))
                acc_full(b, chunk, last_tile)
                V.scalar_tensor_tensor(out=stage[:, b, :], in0=acc[:, b, :], scalar=rfac[:, R_FFN, b:b + 1],
                                       in1=silu_g[:, b, :], op0=ALU.mult, op1=ALU.mult).then_inc(stage_full, 1)
                dve.wait_ge(stage_full, 2 * n + (2 * S_I + b + 1))
                dve.sem_inc(acc_free[b], 1)

            def act_lo(n, count):
                for g in range(2):
                    turned_lo_part(g, count + (g + 1), [[actT[j][:, cols(n * 4 + 2 * g, 2), :]] for j in range(2)])

            for t in range(16):
                if t == 0:
                    mean_square(R_FFN, D, 4, Z_H + 8)
                if t == 14:
                    dve.wait_ge(x_new, 8)
                    dve.wait_ge(r_ready, R_FFN + 1)
                for b in range(NB) if t == 14 else ():
                    gated_up(b, 0, C_I + 1, T_I + 16, 2 * (Q_H + 4))
                split_lo(T_I, t + 4)
                if t == 1:
                    new_x_lo(3, "norm_ffn", H_H + 6)
            with dve.Fori(1, D_FF // CH) as i:
                for t in range(16):
                    for b in range(NB) if t == 14 else ():
                        gated_up(b, i, 2 * i + (C_I + 1), i * 16 + (T_I + 16), 2 * i + 2 * Q_I)
                    split_lo(i * 16 + T_I, t + 4)
                    if t == 1:
                        act_lo(i - 1, 2 * i + (H_I - 2))

            def down(c, first, end):
                for t in range(24):
                    for b in range(NB) if t == 22 else ():
                        acc_full(b, c + C_J, c * 24 + (T_J + 24))
                        V.tensor_tensor(xs[:, b, cols(c * CH, CH)], acc[:, b, :], xs[:, b, cols(c * CH, CH)],
                                        ALU.add).then_inc(x_done, 1)
                        dve.wait_ge(x_done, 2 * c + (b + 1))
                        dve.sem_inc(acc_free[b], 1)
                    if t + 4 < 24 or not end:
                        split_lo(c * 24 + T_J, t + 4, down_tile((t + 4) % 24)[1] * CH)
                    if first and t == 1:
                        act_lo(10, H_I + 20)

            down(0, True, False)
            with dve.Fori(1, 3) as c:
                down(c, False, False)
            down(3, False, True)
            for b in range(NB):
                dve.wait_ge(square_sum, Z_J + 7 + b)
                V.tensor_reduce(ssum[:, R_FIN, b:b + 1], sq[:, R_FIN, b, :], AX.X, ALU.add).then_inc(sums_step, 1)
                sums[0] += 1
                dve.wait_ge(sums_step, sums[0])
                V.tensor_scalar(mean_sq[:, R_FIN, b:b + 1], ssum[:, R_FIN, b:b + 1], 1.0 / D, EPS, ALU.mult, ALU.add)\
                    .then_inc(ms_ready, 1)
            dve.wait_ge(gain_in, 16)
            dve.wait_ge(gained, 3)
            for b in range(NB):
                dve.wait_ge(r_ready, R_FIN + 1 + b)
                V.tensor_scalar(xs[:, b, 2 * CH:3 * CH], xs[:, b, 2 * CH:3 * CH], rfac[:, R_FIN, b:b + 1], None,
                                ALU.mult).then_inc(y_right, 1)
                V.scalar_tensor_tensor(out=xs[:, b, 3 * CH:], in0=xs[:, b, 3 * CH:], scalar=rfac[:, R_FIN, b:b + 1],
                                       in1=row_bc[:, 3 * CH:], op0=ALU.mult, op1=ALU.mult).then_inc(y_right, 1)

        @block.gpsimd
        def _(gp):
            G = nc.gpsimd
            G.memset(ident[:, :], 0.0).then_inc(ident_made, 1)
            gp.wait_ge(ident_made, 1)
            G.affine_select(out=ident[:, :], in_=ident[:, :], compare_op=ALU.not_equal, fill=1.0, base=0,
                            pattern=[[-1, P]], channel_multiplier=1).then_inc(ident_made, 1)
            G.memset(minus_half[:, :], -0.5).then_inc(consts_made, 1)
            for j in range(ROPE // 2):
                ins = G.memset(inv_freq[:, j:j + 1], INV_FREQ[j])
            ins.then_inc(freq_made, 1)

            for name, rows in VECS[1:]:
                gp.dma_start(vec_rows[ROW[name]:ROW[name] + rows, :],
                             vec_dram[name].rearrange("o (r p) -> (o r) p", p=P)).then_inc(vec_in, 16)
            gp.dma_start(ln_tok[0:TAPS, 0, :], w_dw[0, :, :]).then_inc(wdw_in, 16)

            steps = [0]

            def step(ins):
                steps[0] += 1
                ins.then_inc(trig_step, 1)
                gp.wait_ge(trig_step, steps[0])

            gp.wait_ge(pos_in, 16)
            gp.wait_ge(freq_made, 1)
            step(G.tensor_copy(pos_f[:, :], pos_i[:, :]))
            for b in range(NB):
                ins = G.tensor_scalar(ang[:, b, :], inv_freq[:, :], pos_f[:, b:b + 1], None, ALU.mult)
            step(ins)
            two_pi = 2 * math.pi
            c1 = 6.28125
            c2 = float.fromhex("0x1.fb4p-10")
            c3 = two_pi - c1 - c2
            big = 1.5 * 2.0 ** 23
            for f in range(2):
                ins = G.tensor_scalar(turns[:, f, :, :], ang[:, :, :], 1.0 / two_pi, 0.25 * f, ALU.mult, ALU.add)
            step(ins)
            step(G.tensor_scalar(turns[:, :, :, :], turns[:, :, :, :], big, None, ALU.add))
            step(G.tensor_scalar(turns[:, :, :, :], turns[:, :, :, :], big, None, ALU.subtract))
            step(G.tensor_scalar(trig[:, :, :, :], turns[:, :, :, :], c1, None, ALU.mult))
            for f in range(2):
                ins = G.tensor_tensor(resid[:, f, :, :], ang[:, :, :], trig[:, f, :, :], ALU.subtract)
            step(ins)
            for part in (c2, c3):
                step(G.tensor_scalar(trig[:, :, :, :], turns[:, :, :, :], part, None, ALU.mult))
                step(G.tensor_tensor(resid[:, :, :, :], resid[:, :, :, :], trig[:, :, :, :], ALU.subtract))
            step(G.tensor_scalar(resid[:, 1, :, :], resid[:, 1, :, :], math.pi / 2, None, ALU.add))
            lim = 3.1415925
            G.tensor_scalar(resid[:, :, :, :], resid[:, :, :, :], lim, -lim, ALU.min, ALU.max).then_inc(angles_ready, 1)

            G.memset(mask[:, :], 0.0).then_inc(consts_made, 1)
            gp.wait_ge(consts_made, 2)
            G.memset(mask[0:64, 64:P], NEG).then_inc(consts_made, 1)
            G.memset(mask[0:64, P + 192:P + TOK], NEG).then_inc(consts_made, 1)
            gp.wait_ge(consts_made, 4)
            G.memset(uT[:, :, 0:TAPS - 1], 0.0).then_inc(zeros_made, 1)

            def row_factor(norm):
                gp.wait_ge(ms_ready, norm + 1)
                G.tensor_tensor(rfac[:, norm, :], mean_sq[:, norm, :], minus_half[:, :], ALU.pow).then_inc(r_ready, 1)

            def rope(src, dst, heads, wait, before, done):
                def tab(f):
                    return trig[:, f, :, None, :].broadcast_to([P, NB, heads, 32])
                a1, a2 = (rope_a[:, :, 0:heads, 32 * k:32 * k + 32] for k in range(2))
                b1, b2 = (rope_b[:, :, 0:heads, 32 * k:32 * k + 32] for k in range(2))
                G.tensor_tensor(a1, src[0], tab(1), ALU.mult)
                G.tensor_tensor(a2, src[0], tab(0), ALU.mult)
                G.tensor_tensor(b1, src[1], tab(0), ALU.mult)
                G.tensor_tensor(b2, src[1], tab(1), ALU.mult).then_inc(wait, 1)
                gp.wait_ge(wait, before + 1)
                G.tensor_tensor(dst[0], a1, b1, ALU.subtract)
                return G.tensor_tensor(dst[1], a2, b2, ALU.add)

            row_factor(R_X)
            row_factor(R_CQ)
            gp.wait_ge(turned, 8)
            gp.wait_ge(square_sum, Z_X + 8)

            def load_memory(c):
                gp.dma_start(xs[:, :, c * CH:(c + 1) * CH], mem_v[:, :, c * CH:(c + 1) * CH]).then_inc(mem_in, 16)

            load_memory(0)
            gp.wait_ge(stage_full, 4)
            gp.wait_ge(trig_ready, 1)
            key = [stage[:, :, KV_LORA + 32 * k:KV_LORA + 32 * k + 32][:, :, None, :] for k in range(2)]
            rope(key, [qr_tok[:, :, 0:1, 32 * k:32 * k + 32] for k in range(2)], 1, kr_step, 0, None)\
                .then_inc(kr_step, 1)
            gp.wait_ge(kr_step, 2)
            G.tensor_copy(qr_tok[:, :, 1, :], qr_tok[:, :, 0, :]).then_inc(kr_ready, 1)
            row_factor(R_CKV)
            gp.dma_start(row_bc[:, :], b_pw2.broadcast_to([P, D])).then_inc(row_in, 16)
            for c in range(1, 4):
                gp.wait_ge(tile_done, T_B + 4 * c)
                load_memory(c)
            row_factor(R_MEM)
            gp.wait_ge(kr_ready, 1)
            gp.wait_ge(turned, 2 * Q_CKV + 2)

            def query_rope(p, first):
                gp.wait_ge(q_ready, 2 * p + 2)
                if not first:
                    gp.wait_ge(qr_turned, p)
                q = [q_tok[:, :, :, NOPE + 32 * k:NOPE + 32 * k + 32] for k in range(2)]
                rope(q, [qr_tok[:, :, :, 32 * k:32 * k + 32] for k in range(2)], 2, rope_step, p, None)\
                    .then_inc(rope_ready, 1)

            query_rope(0, True)
            with gp.Fori(1, PAIRS) as i:
                gp.wait_ge(rope_ready, i)
                query_rope(i, False)
            gp.wait_ge(turned, 2 * (Q_M1 + 2))
            for c in range(4):
                gp.wait_ge(tile_done, T_E + 8 * c + 8)
                gp.dma_start(xs[:, :, c * CH:(c + 1) * CH], x_v[:, :, c * CH:(c + 1) * CH]).then_inc(x_back, 16)
            row_factor(R_LN)
            for first_fill, norm in ((S_F, R_CROSS), (S_H, R_FFN)):
                with gp.Fori(0, 4) as c:
                    at = gp.snap(c * CH)
                    gp.wait_ge(stage_full, 2 * c + (2 * first_fill + 2))
                    G.tensor_copy(xs[:, :, ds(at, CH)], stage[:, :, :]).then_inc(x_new, 1)
                row_factor(norm)
            gp.wait_ge(stage_full, 2 * (S_I + D_FF // CH))
            gp.dma_start(row_bc[:, :], norm_final.rearrange("(o n) -> o n", o=1).broadcast_to([P, D]))\
                .then_inc(gain_in, 16)
            gp.wait_ge(gain_in, 16)
            for c in range(3):
                gp.wait_ge(square_sum, Z_J + 2 * c + 2)
                at = slice(c * CH, (c + 1) * CH)
                G.tensor_tensor(xs[:, :, at], xs[:, :, at], row_bc[:, None, at].broadcast_to([P, NB, CH]),
                                ALU.mult).then_inc(gained, 1)
            for b in range(NB):
                gp.wait_ge(ms_ready, R_FIN + 1 + b)
                G.tensor_tensor(rfac[:, R_FIN, b:b + 1], mean_sq[:, R_FIN, b:b + 1], minus_half[:, b:b + 1], ALU.pow)\
                    .then_inc(r_ready, 1)


INV_FREQ = [float(f) for f in
            np.float32(1) / np.float32(10000) ** (np.arange(0, ROPE, 2, dtype=np.float32) / np.float32(ROPE))]


_INS = ["x", "mem", "positions", "norm_mix", "w_in", "b_conv_in", "norm_cq", "w_uq", "norm_ckv", "w_ukv",
        "w_dw", "b_dw", "ln_conv_g", "ln_conv_b", "w_pw2", "b_pw2", "w_o", "norm_cross", "norm_mem",
        "w_q_mem", "w_kv_mem", "w_o_mem", "norm_ffn", "w_gate", "w_up", "w_down", "norm_final"]


def kernel(**inputs):
    import numpy as _np
    import concourse.bacc as _bacc
    from concourse import mybir as _mybir
    from concourse.bass_utils import run_bass_kernel_spmd as _run

    nc = _bacc.Bacc("TRN2", target_bir_lowering=False, num_devices=1)
    arrays, args = {}, []
    for name in _INS:
        a = _np.ascontiguousarray(inputs[name])
        arrays[f"in_{name}_dram"] = a
        args.append(nc.dram_tensor(f"in_{name}_dram", a.shape, _mybir.dt.from_np(a.dtype), kind="ExternalInput").ap())
    args.append(nc.dram_tensor("out_0_dram", (1, TOK, D), F32, kind="ExternalOutput").ap())
    program(nc, *args)
    r = _run(nc, [arrays], core_ids=[0])
    return r.results[0]["out_0_dram"]
```
